# Optimizing a Trainium2 kernel written in Bass

```python
import functools
import jax, jax.numpy as jnp
from jax import lax
import numpy as np

D_MODEL = 1024
BATCH = 1
SEQ = 1024
DEPTH = 1
DEC_BATCH = 8
DEC_SEQ = 8
PAST_LEN = 4096
PAGE_SIZE = 128

N_HEADS = 8
HEAD_DIM = 64
N_KV_HEADS = 2
GROUP = N_HEADS // N_KV_HEADS
ATTN_DIM = N_HEADS * HEAD_DIM
KV_DIM = N_KV_HEADS * HEAD_DIM
N_IDX_HEADS = 4
IDX_DIM = 64
TOPK_MAX = 256
CONV_DIM = D_MODEL - ATTN_DIM
CONV_WIDTH = 3
MIX_DIM = ATTN_DIM + CONV_DIM
D_FF = 2816
PLE_DIM = 256
ROPE_THETA = 10000.0
RMS_EPS = 1e-6
Q_BLOCK = 128
_SPLITS = (ATTN_DIM, KV_DIM, KV_DIM, N_IDX_HEADS * IDX_DIM, IDX_DIM, N_IDX_HEADS, CONV_DIM, CONV_DIM, CONV_DIM)
PROJ_DIM = ATTN_DIM + 2 * KV_DIM + N_IDX_HEADS * IDX_DIM + IDX_DIM + N_IDX_HEADS + 3 * CONV_DIM

kernel_name = 'hybrid_dsa_shortconv_macaron_step'

def rms_norm(x, g):
    xf = x.astype(jnp.float32)
    y = xf * lax.rsqrt(jnp.mean(xf * xf, axis=-1, keepdims=True) + RMS_EPS)
    return (y * g.astype(jnp.float32)).astype(x.dtype)

def swiglu(h, w_gate, w_up, w_down):
    return (jax.nn.silu(h @ w_gate) * (h @ w_up)) @ w_down

def rope(x, pos):
    half = x.shape[-1] // 2
    inv = ROPE_THETA ** (-jnp.arange(half, dtype=jnp.float32) / half)
    ang = pos.astype(jnp.float32)[:, None] * inv[None, :]
    cos = jnp.cos(ang)[:, None, :]
    sin = jnp.sin(ang)[:, None, :]
    xf = x.astype(jnp.float32)
    x1, x2 = xf[..., :half], xf[..., half:]
    return jnp.concatenate([x1 * cos - x2 * sin, x2 * cos + x1 * sin], axis=-1).astype(x.dtype)

def split_proj(z):
    parts, o = [], 0
    for w in _SPLITS:
        parts.append(z[..., o:o + w])
        o += w
    return parts

def project_heads(z, pos):
    q, k, v, iq, ik, iw, cb, cc, ch = split_proj(z)
    b, t = z.shape[0], z.shape[1]
    q = rope(q.reshape(b, t, N_HEADS, HEAD_DIM), pos)
    k = rope(k.reshape(b, t, N_KV_HEADS, HEAD_DIM), pos)
    v = v.reshape(b, t, N_KV_HEADS, HEAD_DIM)
    iq = rope(iq.reshape(b, t, N_IDX_HEADS, IDX_DIM), pos)
    ik = rope(ik.reshape(b, t, 1, IDX_DIM), pos)[:, :, 0]
    return q, k, v, iq, ik, iw, cb, cc, ch

def indexer_select(iq, iw, ik, qpos, topk):
    logits = jnp.einsum('bthd,bld->bthl', iq.astype(jnp.float32), ik.astype(jnp.float32)) * (IDX_DIM ** -0.5)
    w = iw.astype(jnp.float32) * (N_IDX_HEADS ** -0.5)
    score = jnp.einsum('bth,bthl->btl', w, jax.nn.relu(logits))
    adm = jnp.arange(ik.shape[1])[None, :] <= qpos[:, None]
    score = jnp.where(adm[None], score, -jnp.inf)
    _, idx = lax.top_k(score, topk)
    valid = idx <= qpos[None, :, None]
    return idx, valid

def gqa_attend(q, k_sel, v_sel, valid):
    b, t = q.shape[0], q.shape[1]
    qg = q.reshape(b, t, N_KV_HEADS, GROUP, HEAD_DIM).astype(jnp.float32)
    s = jnp.einsum('btngd,btknd->btngk', qg, k_sel.astype(jnp.float32)) * (HEAD_DIM ** -0.5)
    s = jnp.where(valid[:, :, None, None, :], s, -jnp.inf)
    p = jax.nn.softmax(s, axis=-1)
    o = jnp.einsum('btngk,btknd->btngd', p, v_sel.astype(jnp.float32))
    return o.reshape(b, t, ATTN_DIM).astype(q.dtype)

def short_conv(cb, cc, ch, buf, conv_w):
    u = cc * ch
    t = u.shape[1]
    up = jnp.concatenate([buf.astype(u.dtype), u], axis=1)
    y = conv_w[0] * up[:, 0:t]
    for j in range(1, CONV_WIDTH):
        y = y + conv_w[j] * up[:, j:j + t]
    return cb * y, up[:, t:]

def prompt_mixer(z, conv_w):
    b, s = z.shape[0], z.shape[1]
    pos = jnp.arange(s, dtype=jnp.int32)
    q, k, v, iq, ik, iw, cb, cc, ch = project_heads(z, pos)
    topk = min(TOPK_MAX, s // 4)
    nb = s // Q_BLOCK
    bidx = jnp.arange(b)[:, None, None]

    def to_blocks(a):
        return jnp.moveaxis(a.reshape((b, nb, Q_BLOCK) + a.shape[2:]), 1, 0)

    def block(args):
        qb, iqb, iwb, qpos = args
        idx, valid = indexer_select(iqb, iwb, ik, qpos, topk)
        return gqa_attend(qb, k[bidx, idx], v[bidx, idx], valid)

    attn = lax.map(block, (to_blocks(q), to_blocks(iq), to_blocks(iw), pos.reshape(nb, Q_BLOCK)))
    attn = jnp.moveaxis(attn, 0, 1).reshape(b, s, ATTN_DIM)
    buf = jnp.zeros((b, CONV_WIDTH - 1, CONV_DIM), z.dtype)
    conv_out, conv_state = short_conv(cb, cc, ch, buf, conv_w)
    return jnp.concatenate([attn, conv_out], axis=-1), (k, v, ik, conv_state)

def sample_mixer(z, conv_w, cache_k, cache_v, cache_idx_k, conv_buf, page_table):
    db, t = z.shape[0], z.shape[1]
    past = page_table.shape[1] * PAGE_SIZE
    pos = past + jnp.arange(t, dtype=jnp.int32)
    q, k, v, iq, ik, iw, cb, cc, ch = project_heads(z, pos)
    topk = min(TOPK_MAX, (past + t) // 4)
    ik_past = cache_idx_k[page_table].reshape(db, past, IDX_DIM)
    ik_all = jnp.concatenate([ik_past.astype(ik.dtype), ik], axis=1)
    idx, valid = indexer_select(iq, iw, ik_all, pos, topk)
    bidx = jnp.arange(db)[:, None, None]
    is_past = (idx < past)[..., None, None]
    pidx = jnp.minimum(idx, past - 1)
    phys = page_table[bidx, pidx // PAGE_SIZE]
    off = pidx % PAGE_SIZE
    nidx = jnp.clip(idx - past, 0, t - 1)

    def select_rows(cache, new):
        return jnp.where(is_past, cache[phys, off].astype(new.dtype), new[bidx, nidx])

    attn = gqa_attend(q, select_rows(cache_k, k), select_rows(cache_v, v), valid)
    conv_out, conv_state = short_conv(cb, cc, ch, conv_buf, conv_w)
    return jnp.concatenate([attn, conv_out], axis=-1), (k, v, ik, conv_state)

def decoder_layer(x, pe, mixer, g_ffn1, w1_gate, w1_up, w1_down, g_mix, w_in, w_out,
                  g_ffn2, w2_gate, w2_up, w2_down, g_ple, w_ple_gate, w_ple_proj):
    x = x + 0.5 * swiglu(rms_norm(x, g_ffn1), w1_gate, w1_up, w1_down)
    mixed, state = mixer(rms_norm(x, g_mix) @ w_in)
    x = x + mixed @ w_out
    x = x + 0.5 * swiglu(rms_norm(x, g_ffn2), w2_gate, w2_up, w2_down)
    gate = jax.nn.sigmoid(rms_norm(x, g_ple) @ w_ple_gate)
    x = x + gate * (pe @ w_ple_proj)
    return x, state

def setup_inputs(seed: int = 0) -> dict:
    key = jax.random.key(seed)
    ks = jax.random.split(key, 32)
    f32 = jnp.float32
    n_pages = PAST_LEN // PAGE_SIZE
    n_pool = (DEC_BATCH * n_pages * 5) // 4

    def nrm(k, shape, scale):
        return jax.random.normal(k, shape, f32) * scale

    def gain(k, shape):
        return 1.0 + 0.05 * jax.random.normal(k, shape, f32)

    page_table = jax.random.permutation(ks[0], n_pool)[:DEC_BATCH * n_pages].reshape(DEC_BATCH, n_pages).astype(jnp.int32)
    return {
        'x_prompt': nrm(ks[1], (BATCH, SEQ, D_MODEL), 1.0),
        'x_sample': nrm(ks[2], (DEC_BATCH, DEC_SEQ, D_MODEL), 1.0),
        'cache_k': nrm(ks[3], (DEPTH, n_pool, PAGE_SIZE, N_KV_HEADS, HEAD_DIM), 1.0),
        'cache_v': nrm(ks[4], (DEPTH, n_pool, PAGE_SIZE, N_KV_HEADS, HEAD_DIM), 1.0),
        'cache_idx_k': nrm(ks[5], (DEPTH, n_pool, PAGE_SIZE, IDX_DIM), 1.0),
        'state_conv': nrm(ks[6], (DEPTH, DEC_BATCH, CONV_WIDTH - 1, CONV_DIM), 1.0),
        'page_table': page_table,
        'p_prompt': nrm(ks[7], (DEPTH, BATCH, SEQ, PLE_DIM), 1.0),
        'p_sample': nrm(ks[8], (DEPTH, DEC_BATCH, DEC_SEQ, PLE_DIM), 1.0),
        'g_ffn1': gain(ks[9], (DEPTH, D_MODEL)),
        'w1_gate': nrm(ks[10], (DEPTH, D_MODEL, D_FF), D_MODEL ** -0.5),
        'w1_up': nrm(ks[11], (DEPTH, D_MODEL, D_FF), D_MODEL ** -0.5),
        'w1_down': nrm(ks[12], (DEPTH, D_FF, D_MODEL), D_FF ** -0.5),
        'g_mix': gain(ks[13], (DEPTH, D_MODEL)),
        'w_in': nrm(ks[14], (DEPTH, D_MODEL, PROJ_DIM), D_MODEL ** -0.5),
        'conv_w': nrm(ks[15], (DEPTH, CONV_WIDTH, CONV_DIM), CONV_WIDTH ** -0.5),
        'w_out': nrm(ks[16], (DEPTH, MIX_DIM, D_MODEL), MIX_DIM ** -0.5),
        'g_ffn2': gain(ks[17], (DEPTH, D_MODEL)),
        'w2_gate': nrm(ks[18], (DEPTH, D_MODEL, D_FF), D_MODEL ** -0.5),
        'w2_up': nrm(ks[19], (DEPTH, D_MODEL, D_FF), D_MODEL ** -0.5),
        'w2_down': nrm(ks[20], (DEPTH, D_FF, D_MODEL), D_FF ** -0.5),
        'g_ple': gain(ks[21], (DEPTH, D_MODEL)),
        'w_ple_gate': nrm(ks[22], (DEPTH, D_MODEL, D_MODEL), D_MODEL ** -0.5),
        'w_ple_proj': nrm(ks[23], (DEPTH, PLE_DIM, D_MODEL), PLE_DIM ** -0.5),
        'g_final': gain(ks[24], (D_MODEL,)),
    }

def reference(x_prompt, x_sample, cache_k, cache_v, cache_idx_k, state_conv, page_table, p_prompt, p_sample,
              g_ffn1, w1_gate, w1_up, w1_down, g_mix, w_in, conv_w, w_out,
              g_ffn2, w2_gate, w2_up, w2_down, g_ple, w_ple_gate, w_ple_proj, g_final):
    xp, xs = x_prompt, x_sample
    p_states, s_states = [], []
    for i in range(DEPTH):
        shared = (g_ffn1[i], w1_gate[i], w1_up[i], w1_down[i], g_mix[i], w_in[i], w_out[i],
                  g_ffn2[i], w2_gate[i], w2_up[i], w2_down[i], g_ple[i], w_ple_gate[i], w_ple_proj[i])
        xp, st_p = decoder_layer(xp, p_prompt[i], functools.partial(prompt_mixer, conv_w=conv_w[i]), *shared)
        xs, st_s = decoder_layer(
            xs, p_sample[i],
            functools.partial(sample_mixer, conv_w=conv_w[i], cache_k=cache_k[i], cache_v=cache_v[i],
                              cache_idx_k=cache_idx_k[i], conv_buf=state_conv[i], page_table=page_table),
            *shared)
        p_states.append(st_p)
        s_states.append(st_s)
    y_prompt = rms_norm(xp, g_final)
    y_sample = rms_norm(xs, g_final)
    k_prompt, v_prompt, idx_k_prompt, conv_prompt = (jnp.stack(a) for a in zip(*p_states))
    k_sample, v_sample, idx_k_sample, conv_sample = (jnp.stack(a) for a in zip(*s_states))
    return (y_prompt, y_sample, k_prompt, v_prompt, idx_k_prompt, conv_prompt,
            k_sample, v_sample, idx_k_sample, conv_sample)


_drawn_inputs = setup_inputs


def setup_inputs(seed=0):
    import zlib

    import numpy as np

    out = dict(_drawn_inputs(seed))
    spreads = {}
    factors = {'g_ffn2': 3.735, 'g_ple': 7.362}
    for name, (base, spread) in spreads.items():
        noise = np.random.default_rng([zlib.crc32(name.encode()), seed]).standard_normal(out[name].shape)
        drawn = base * np.exp(spread * noise) if base else spread * noise
        out[name] = __import__('jax').numpy.asarray(drawn.astype(out[name].dtype))
    for name, factor in factors.items():
        out[name] = (out[name] * factor).astype(out[name].dtype)
    return out
```

```python
import numpy as np
import concourse.bass as bass
from concourse import mybir
from contextlib import ExitStack

f32, f32r, bf16, i32 = mybir.dt.float32, mybir.dt.float32r, mybir.dt.bfloat16, mybir.dt.int32
ALU, ACT, AX = mybir.AluOpType, mybir.ActivationFunctionType, mybir.AxisListType

D, FF = 1024, 2816
SEQ, NB, DT = 1024, 8, 8
T = SEQ + NB * DT
KT, FT = D // 128, FF // 128
PAIRS = FT // 2
PAST, PAGE = 4096, 128
PAGES = PAST // PAGE
NPOOL = NB * PAGES * 5 // 4
TOPK = 256
HALF = PAST // 2
HW = HALF + DT
NS = PAST + DT
CH = [(0, 364), (364, 362), (726, 362)]
N_IN, N_OUT, N_PLE = 21, 8, 8
T_K, T_Q, T_V, T_CONV = 3, 4, 8, 9
NEG = -3.0e38
STRUCK = -3.3e38
OFF = -float(2 ** 100)
W_READY = 16 + 1


def program(nc, x_in, consts_in, ident_in, sel_in, wg_in, ptab_in, rope_in, w_gu, w_d, w_ring, w_iw, w_pp,
            idx_pages, kv_pages, p_in, y_out, k_out, v_out, ik_out, conv_out, x_spill, idx_flat):
    ctx = ExitStack()
    with ctx:
        def at(name, shape, dt, offset):
            return nc.alloc_sbuf_tensor_at(name, shape, dt, offset=16512 + offset)

        def sem(name):
            return ctx.enter_context(nc.semaphore(name))

        ones = at("ones", [128, 128], f32, 0)
        consts = at("consts", [128, 64], f32, 512)
        eps = at("eps", [128, 1], f32, 768)
        zero = at("zero", [128, 1], f32, 800)
        ident = at("ident", [128, 2, 128], f32, 832)
        tri = ident[:, 1, :]
        sel = at("sel", [128, NB, 64], bf16, 1856)
        conv_st = at("conv_st", [128, 4, NB, 2], f32, 2880)
        iw = at("iw", [128, 9, 4], f32, 3136)
        conv_new = at("conv_new", [128, 4, 18], f32, 3296)
        ptab = at("ptab", [1, NB * PAGES], i32, 3584)
        m8 = at("m8", [128, 8], f32, 4608)
        mx = at("mx", [128, 2], f32, 4640)
        nb = at("nb", [128, 2], f32, 4672)
        rs = at("rs", [128, 2], f32, 4704)
        ri = at("ri", [128, 2], f32, 4736)
        mx9 = at("mx9", [64, 2, 9], f32, 4768)
        tau = at("tau", [128, 1], f32, 4864)
        cnt = at("cnt", [128, 8], f32, 4896)
        cstmp = at("cstmp", [128, 2, NB, 2], f32, 4928)
        wgt = at("wgt", [128, 2, 128], f32, 5056)
        x = at("x", [128, KT, T], f32, 6144)
        convf = at("convf", [128, 4, T], f32, 6144)
        tb = [at(f"tb{i}", [128, T], f32, 23552 + 4352 * i) for i in range(4)]
        attn = at("attn", [128, 4, T], f32, 23552)
        xn_hi = at("xn_hi", [128, KT, T], f32r, 40960)
        xn_lo = at("xn_lo", [128, KT, T], f32r, 75776)
        h_hi = at("h_hi", [128, 2, T], f32r, 110592)
        h_lo = at("h_lo", [128, 2, T], f32r, 119296)
        gu_hi = [at(f"gu_hi{s}", [128, 2, KT, 128], f32r, 128000 + 8192 * s) for s in range(2)]
        gu_lo = [at(f"gu_lo{s}", [128, 2, KT, 128], f32r, 144384 + 8192 * s) for s in range(2)]
        d_hi = at("d_hi", [128, 2, D], f32r, 160768)
        d_lo = at("d_lo", [128, 2, D], f32r, 168960)
        raw_gu = at("raw_gu", [128, 2, KT, 128], f32, 177152)
        raw_d = at("raw_d", [128, D], f32, 185344)
        silu = at("silu", [128, 3, 364], f32, 189440)
        hf = at("hf", [128, 3, 364], f32, 193824)
        sq = at("sq", [128, KT, 364], f32, 198208)
        ssum = at("ssum", [128, 364], f32, 209856)
        rms = at("rms", [128, 364], f32, 211328)
        wi_hi = [at(f"wi_hi{s}", [128, KT, 128], f32r, 110592 + 4096 * s) for s in range(2)]
        wi_lo = [at(f"wi_lo{s}", [128, KT, 128], f32r, 118784 + 4096 * s) for s in range(2)]
        wraw = [at(f"wraw{s}", [128, KT, 128], f32, 126976 + 4096 * s) for s in range(2)]
        rope = at("rope", [128, 2, T], f32, 135168)
        qT = at("qT", [128, 4, T], f32, 143872)
        kT = at("kT", [128, T], f32, 161280)
        iqT = at("iqT", [128, 2, T], f32, 165632)
        ikT = at("ikT", [128, T], f32, 174336)
        iw_raw = at("iw_raw", [128, KT, 4], f32, 178688)
        iw_hi = at("iw_hi", [128, KT, 4], f32r, 178816)
        iw_lo = at("iw_lo", [128, KT, 4], f32r, 178944)
        V = at("V", [128, 8, 128], f32, 178688)
        vT = at("vT", [128, T], f32, 182784)
        scores = at("scores", [128, 4608], f32, 187136)
        rl = at("rl", [128, 2, 512], f32, 205568)
        iqbd = at("iqbd", [128, 4, 64], f32, 209664)
        ikn = at("ikn", [128, 4, DT], f32, 210688)
        Wm = at("Wm", [128, 2, 64], f32, 210816)
        WT = at("WT", [128, 2, 128], f32, 211328)
        kn = at("kn", [128, NB * DT], f32, 212352)
        idxp = [at(f"idxp{s}", [128, 4, 512], f32, 40960 + 8192 * s) for s in range(2)]
        R = [at(f"R{s}", [128, 2, 512], f32, 57344 + 4096 * s) for s in range(2)]
        S0 = at("S0", [128, HW], f32, 65536)
        Wk = at("Wk", [128, HW], f32, 73760)
        eqb = at("eqb", [128, HW], bf16, 81984)
        cum = at("cum", [128, HW], f32, 86112)
        vals = at("vals", [128, TOPK], f32, 94336)
        valsB = at("valsB", [64, TOPK], f32, 95360)
        smask = at("smask", [128, HW], bf16, 96384)
        qbd = at("qbd", [128, NB, 64], f32, 100512)
        vn = at("vn", [DT, NB, 128], f32, 102560)
        Sx = [at("Sx0", [128, 1024], f32, 205568), at("Sx1", [128, 1024], f32, 40960)]
        PT = [at("PT0", [128, 8, 128], f32, 45056), at("PT1", [128, 8, 128], f32, 49152)]
        Sa = [at(f"Sa{s}", [64, NS], f32, 40960 + 16416 * s) for s in range(2)]
        PTa = [at(f"PTa{s}", [128, PAGES + 1, 64], f32, 73792 + 8448 * s) for s in range(2)]
        kv = [at(f"kv{s}", [128, PAGES, 256], f32, 110592 + 32768 * s) for s in range(3)]
        xr = at("xr", [128, KT, T], f32, 176640 + 512)
        pe_raw = at("pe_raw", [128, 2, T], f32, 135168)
        pe_hi = at("pe_hi", [128, 2, T], f32r, 143872)
        pe_lo = at("pe_lo", [128, 2, T], f32r, 152576)
        pp_raw = [at(f"pp_raw{s}", [128, 2, 128], f32, 161280 + 1024 * s) for s in range(2)]
        pp_hi = [at(f"pp_hi{s}", [128, 2, 128], f32r, 163328 + 1024 * s) for s in range(2)]
        pp_lo = [at(f"pp_lo{s}", [128, 2, 128], f32r, 165376 + 1024 * s) for s in range(2)]
        y = at("y", [128, KT, T], f32, 40960)

        ps = ctx.enter_context(nc.psum_tensor("ps", [128, 8, 512], f32))

        gain = lambda k, kt: consts[:, k * KT + kt:k * KT + kt + 1]
        tap = lambda j, w: consts[:, 40 + 3 * j + w:41 + 3 * j + w]
        causal8 = consts[64:128, 52:60]

        def block_cols(b):
            o = 128 * (b * (b + 1) // 2)
            return scores[:, o:o + 128 * (b + 1)]

        x_loaded = [sem(f"x_loaded{c}") for c in range(3)]
        consts_loaded, sel_loaded, sel_ready, memset_done = sem("consts_loaded"), sem("sel_loaded"), sem("sel_ready"), sem("memset_done")
        sq_done, ssum_done, tot_done, rms_done = sem("sq_done"), sem("ssum_done"), sem("tot_done"), sem("rms_done")
        recip_done, xnf_done, xn_hi_done, xn_ready = sem("recip_done"), sem("xnf_done"), sem("xn_hi_done"), sem("xn_ready")
        F = []
        for f in range(2):
            F.append({n: sem(f"ffn{f}_{n}") for n in (
                "gu_loaded", "d_loaded", "gu_hi_done", "gu_ready", "d_hi_done", "d_ready", "gate_done", "up_done",
                "silu_done", "hmul_done", "h_hi_done", "h_ready", "down_done", "acc_done")})
        idx_gathered, x_spilled, rope_loaded, iw_loaded = sem("idx_gathered"), sem("x_spilled"), sem("rope_loaded"), sem("iw_loaded")
        wi_loaded = [sem(f"wi_loaded{s}") for s in range(2)]
        wi_hi_done, wi_ready, z_done, z_free = sem("wi_hi_done"), sem("wi_ready"), sem("z_done"), sem("z_free")
        iw_hi_done, iw_ready, iw_done, iw_copied = sem("iw_hi_done"), sem("iw_ready"), sem("iw_done"), sem("iw_copied")
        rope_step, rope_dve = sem("rope_step"), sem("rope_dve")
        rope_pstep, rope_pool, conv_step, conv_done = sem("rope_pstep"), sem("rope_pool"), sem("conv_step"), sem("conv_done")
        idx_mm, idx_relu, idx_acc = sem("idx_mm"), sem("idx_relu"), sem("idx_acc")
        prep_zero, prep_dve, wt_done, wm_t, wm_ready = sem("prep_zero"), sem("prep_dve"), sem("wt_done"), sem("wm_t"), sem("wm_ready")
        kn_ready, qbd_zero, qbd_ready, s0_pad = sem("kn_ready"), sem("qbd_zero"), sem("qbd_ready"), sem("s0_pad")
        v_t, v_copied = sem("v_t"), sem("v_copied")
        idx_loaded = [sem(f"idx_loaded{s}") for s in range(2)]
        si_mm, si_relu, si_w, si_evac = sem("si_mm"), sem("si_relu"), sem("si_w"), sem("si_evac")
        top_step = sem("top_step")
        qk_done, smax_done, nb_done, exp_done, ri_done, norm_done = sem("qk_done"), sem("smax_done"), sem("nb_done"), sem("exp_done"), sem("ri_done"), sem("norm_done")
        tr_done, pt_done, pv_done, o_done, mask_ready = sem("tr_done"), sem("pt_done"), sem("pv_done"), sem("o_done"), sem("mask_ready")
        stop_step, smask_ready = sem("stop_step"), sem("smask_ready")
        kv_loaded = [sem(f"kv_loaded{s}") for s in range(3)]
        s_mm, s_evac, s_mx, s_nb, s_exp, s_ri, s_norm = sem("s_mm"), sem("s_evac"), sem("s_mx"), sem("s_nb"), sem("s_exp"), sem("s_ri"), sem("s_norm")
        s_tr, s_pt, s_pv, s_o = sem("s_tr"), sem("s_pt"), sem("s_pv"), sem("s_o")
        xr_loaded, mix_hi, mixa_ready, mixc_ready, wo_added = sem("xr_loaded"), sem("mix_hi"), sem("mixa_ready"), sem("mixc_ready"), sem("wo_added")
        pe_loaded, pe_hi_done, pe_ready = sem("pe_loaded"), sem("pe_hi_done"), sem("pe_ready")
        pp_loaded = [sem(f"pp_loaded{s}") for s in range(2)]
        pp_hi_done, pp_ready = sem("pp_hi_done"), sem("pp_ready")
        pg_done, pj_done, sig_done, pmul_done, ple_done = sem("pg_done"), sem("pj_done"), sem("sig_done"), sem("pmul_done"), sem("ple_done")
        stored = sem("stored")
        y_stored = sem("y_stored")

        def wait(eng, s, v):
            if v > 0:
                eng.wait_ge(s, v)

        def x_final(eng, k, c):
            if k == 0:
                eng.wait_ge(x_loaded[c], 16)
            elif k in (1, 3):
                eng.wait_ge(F[k // 2]["acc_done"], 2 + 24 * (PAIRS - 1) + 8 * (c + 1))
            elif k == 2:
                eng.wait_ge(wo_added, 3 * N_OUT)
            else:
                eng.wait_ge(ple_done, 3 * (N_PLE - 1) + c + 1)

        block = ctx.enter_context(nc.Block())

        @block.sync
        def _(sp):
            for c, (o, n) in enumerate(CH):
                sp.dma_start(x[:, :, o:o + n], x_in[:, :, o:o + n]).then_inc(x_loaded[c], 16)
            for dst, src in ((consts[:, :], consts_in), (ident[:, :, :], ident_in), (ptab[:, :], ptab_in),
                             (conv_st[:, :, :, :], p_in[1]), (wgt[:, :, :], wg_in)):
                sp.dma_start(dst, src).then_inc(consts_loaded, 16)
            sp.dma_start(hf[:, 0:2, 0:256], sel_in).then_inc(sel_loaded, 16)

            def ffn_loads(f, i):
                for s in range(2):
                    sp.wait_ge(F[f]["gu_ready"], i * 2 + (s + 1))
                    sp.dma_start(raw_gu[:, :, :, :], w_gu[f][bass.ds(i * 2 + s, 1)].rearrange("o p a k n -> p (o a) k n")).then_inc(F[f]["gu_loaded"], 16)
                for s in range(2):
                    sp.wait_ge(F[f]["d_ready"], i * 2 + (s + 1))
                    sp.dma_start(raw_d[:, :], w_d[f][bass.ds(i * 2 + s, 1)].rearrange("o p n -> p (o n)")).then_inc(F[f]["d_loaded"], 16)

            sp.wait_ge(consts_loaded, 16 * 5)
            with sp.Fori(0, NB) as i:
                ffn_loads(0, i)
                with sp.Fori(0, PAGES) as j:
                    page = sp.value_load(ptab[0:1, bass.ds(i * PAGES + j, 1)], min_val=0, max_val=NPOOL - 1)
                    sp.dma_start(idx_flat[bass.ds(i, 1), :, bass.ds(j * PAGE, PAGE)],
                                 idx_pages[bass.ds(page, 1)]).then_inc(idx_gathered, 16)
            with sp.Fori(NB, PAIRS) as i:
                ffn_loads(0, i)

            for c, (o, n) in enumerate(CH):
                x_final(sp, 1, c)
                sp.dma_start(x_spill[:, :, o:o + n], x[:, :, o:o + n]).then_inc(x_spilled, 16)
            sp.wait_ge(F[0]["down_done"], W_READY + 24 * PAIRS)
            sp.dma_start(rope[:, :, :], rope_in).then_inc(rope_loaded, 16)

            def ring_load(w):
                wait(sp, wi_ready, w - 1)
                sp.dma_start(wraw[w % 2][:, :, :], w_ring[w]).then_inc(wi_loaded[w % 2], 16)

            ring_load(0)
            sp.dma_start(iw_raw[:, :, :], w_iw).then_inc(iw_loaded, 16)
            for w in range(1, N_IN):
                ring_load(w)
            sp.wait_ge(rope_pool, 1)
            sp.dma_start(k_out, kT[:, :]).then_inc(stored, 16)
            sp.wait_ge(rope_dve, 3)
            sp.dma_start(ik_out, ikT[0:64, :]).then_inc(stored, 16)
            sp.wait_ge(z_free, 3 * T_V + 3)
            sp.dma_start(v_out, vT[:, :]).then_inc(stored, 16)
            sp.wait_ge(z_done, 3 * N_IN)
            sp.wait_ge(idx_gathered, 16 * NB * PAGES)

            def idx_load(kc):
                wait(sp, si_mm, 2 * (kc - 1))
                sp.dma_start(idxp[kc % 2][:, :, :],
                             idx_flat[:, :, kc * 512:kc * 512 + 512].rearrange("(pr b) d k -> (b d) pr k", b=2)).then_inc(idx_loaded[kc % 2], 16)

            for kc in range(8):
                idx_load(kc)

            def kv_load(b):
                with sp.Fori(0, PAGES) as j:
                    page = sp.value_load(ptab[0:1, bass.ds(j + b * PAGES, 1)], min_val=0, max_val=NPOOL - 1)
                    sp.dma_start(kv[b % 3][:, bass.ds(j, 1), :], kv_pages[bass.ds(page, 1)].rearrange("o p n -> p o n")).then_inc(kv_loaded[b % 3], 16)

            sp.wait_ge(rope_pool, 5)
            kv_load(0)
            sp.wait_ge(conv_done, 4)
            sp.dma_start(conv_out, conv_new[:, :, :]).then_inc(stored, 16)
            sp.wait_ge(stored, 64)
            sp.wait_ge(o_done, 32)
            for b in range(1, NB):
                if b >= 3:
                    sp.wait_ge(s_pv, b - 2)
                kv_load(b)
            sp.wait_ge(s_pv, NB - 2)
            sp.wait_ge(x_spilled, 48)
            sp.dma_start(xr[:, :, :], x_spill).then_inc(xr_loaded, 16)
            sp.wait_ge(s_pv, NB - 1)
            for w in range(N_IN, N_IN + N_OUT):
                ring_load(w)

            sp.wait_ge(wo_added, 3 * N_OUT)
            with sp.Fori(0, PAIRS) as i:
                ffn_loads(1, i)
            sp.wait_ge(F[1]["down_done"], W_READY + 24 * PAIRS)
            for w in range(N_IN + N_OUT, N_IN + N_OUT + N_PLE):
                m = w - N_IN - N_OUT
                ring_load(w)
                wait(sp, pp_ready, m - 1)
                sp.dma_start(pp_raw[m % 2][:, :, :], w_pp[m]).then_inc(pp_loaded[m % 2], 16)
                if m == 0:
                    sp.dma_start(pe_raw[:, :, :], p_in[0]).then_inc(pe_loaded, 16)
            for c, (o, n) in enumerate(CH):
                sp.wait_ge(xnf_done, 3 * 4 + c + 1)
                sp.dma_start(y_out[:, :, o:o + n], y[:, :, o:o + n]).then_inc(y_stored, 16)
            sp.wait_ge(y_stored, 48)

        @block.gpsimd
        def _(pool):
            nc.gpsimd.memset(ones[:, :], 1.0)
            nc.gpsimd.memset(zero[:, :], 0.0)
            nc.gpsimd.memset(eps[:, :], 1e-6).then_inc(memset_done, 1)

            def norm_lo(k):
                for c, (o, n) in enumerate(CH):
                    m = 3 * k + c
                    pool.wait_ge(xn_hi_done, m + 1)
                    nc.gpsimd.tensor_tensor(xn_lo[:, :, o:o + n], sq[:, :, 0:n], xn_hi[:, :, o:o + n].bitcast(f32), ALU.subtract).then_inc(xn_ready, 1)

            def ffn(f):
                s_ = F[f]
                pool.drain().then_inc(s_["gu_ready"], 1)
                pool.drain().then_inc(s_["d_ready"], 1)
                with pool.Fori(0, PAIRS) as i:
                    for s in range(2):
                        pool.wait_ge(s_["gu_loaded"], i * 32 + 16 * (s + 1))
                        pool.wait_ge(s_["up_done"], i * 6 + (3 * s + 1))
                        nc.gpsimd.tensor_tensor(gu_hi[s][:, :, :, :], raw_gu[:, :, :, :], zero[:, :].unsqueeze(2).unsqueeze(3).to_broadcast([128, 2, KT, 128]), ALU.add).then_inc(s_["gu_hi_done"], 1)
                        pool.wait_ge(s_["gu_hi_done"], i * 2 + (s + 1))
                        nc.gpsimd.tensor_tensor(gu_lo[s][:, :, :, :], raw_gu[:, :, :, :], gu_hi[s][:, :, :, :].bitcast(f32), ALU.subtract).then_inc(s_["gu_ready"], 1)
                    pool.wait_ge(s_["down_done"], i * 24 + W_READY)
                    for s in range(2):
                        pool.wait_ge(s_["d_loaded"], i * 32 + 16 * (s + 1))
                        nc.gpsimd.tensor_tensor(d_hi[:, s, :], raw_d[:, :], zero[:, :].to_broadcast([128, D]), ALU.add).then_inc(s_["d_hi_done"], 1)
                        pool.wait_ge(s_["d_hi_done"], i * 2 + (s + 1))
                        nc.gpsimd.tensor_tensor(d_lo[:, s, :], raw_d[:, :], d_hi[:, s, :].bitcast(f32), ALU.subtract).then_inc(s_["d_ready"], 1)

            def ring_lo(w):
                pool.wait_ge(wi_hi_done, w + 1)
                nc.gpsimd.tensor_tensor(wi_lo[w % 2][:, :, :], wraw[w % 2][:, :, :], wi_hi[w % 2][:, :, :].bitcast(f32), ALU.subtract).then_inc(wi_ready, 1)

            norm_lo(0)
            ffn(0)
            norm_lo(1)
            pool.wait_ge(xn_ready, 6)
            pool.wait_ge(recip_done, 6)
            pool.wait_ge(xnf_done, 6)
            nc.gpsimd.memset(iqbd[:, :, :], 0.0).then_inc(prep_zero, 1)
            ring_lo(0)
            pool.wait_ge(iw_hi_done, 1)
            nc.gpsimd.tensor_tensor(iw_lo[:, :, :], iw_raw[:, :, :], iw_hi[:, :, :].bitcast(f32), ALU.subtract).then_inc(iw_ready, 1)
            for w in range(1, 5):
                ring_lo(w)

            def step(ins, s, count):
                count[0] += 1
                ins.then_inc(s, 1)
                pool.wait_ge(s, count[0])

            rsteps, csteps = [0], [0]
            g = nc.gpsimd
            for t in range(T_K, N_IN):
                if t in range(T_K, T_V):
                    z, zs = (tb[0], tb[1]) if t % 2 == 0 else (tb[2], tb[3])
                    dst = kT[:, :] if t == T_K else qT[:, t - T_Q, :]
                    pool.wait_ge(z_free, 3 * t + 3)
                    if t == T_K:
                        pool.wait_ge(rope_loaded, 16)
                    g.tensor_tensor(z[:, :], z[:, :], rope[:, 0, :], ALU.mult)
                    step(g.tensor_tensor(zs[:, :], zs[:, :], rope[:, 1, :], ALU.mult), rope_pstep, rsteps)
                    g.tensor_tensor(dst, z[:, :], zs[:, :], ALU.add).then_inc(rope_pool, 1)
                    if t == T_K:
                        pool.wait_ge(rope_pool, 1)
                        g.tensor_copy(kn[:, :], kT[:, SEQ:T]).then_inc(kn_ready, 1)
                if t >= T_CONV and (t - T_CONV) % 3 == 2:
                    j = (t - T_CONV) // 3
                    u, a, yb, cb = tb[0], tb[1], tb[3], tb[2]
                    us = lambda b_: b_[:, SEQ:T].rearrange("p (b t) -> p b t", t=DT)
                    st = lambda ins: step(ins, conv_step, csteps)
                    pool.wait_ge(z_free, 3 * t + 3)
                    st(g.tensor_tensor(u[:, :], u[:, :], a[:, :], ALU.mult))
                    g.tensor_copy(conv_new[:, j, 0:2], u[:, SEQ - 2:SEQ])
                    g.tensor_copy(conv_new[:, j, 2:18].rearrange("p (b t) -> p b t", t=2), us(u)[:, :, DT - 2:DT])
                    for lag in (1, 2):
                        g.tensor_scalar(cstmp[:, lag - 1, :, :], conv_st[:, j, :, :], tap(j, 2 - lag), None, ALU.mult)
                    g.tensor_scalar(yb[:, :], u[:, :], tap(j, 2), None, ALU.mult)
                    for lag in (1, 2):
                        st(g.tensor_scalar(a[:, :], u[:, :], tap(j, 2 - lag), None, ALU.mult))
                        g.tensor_tensor(yb[:, lag:SEQ], yb[:, lag:SEQ], a[:, 0:SEQ - lag], ALU.add)
                        g.tensor_tensor(us(yb)[:, :, lag:DT], us(yb)[:, :, lag:DT], us(a)[:, :, 0:DT - lag], ALU.add)
                        st(g.tensor_tensor(us(yb)[:, :, 0:lag], us(yb)[:, :, 0:lag], cstmp[:, lag - 1, :, 2 - lag:2], ALU.add))
                    g.tensor_tensor(convf[:, j, :], yb[:, :], cb[:, :], ALU.mult).then_inc(conv_done, 1)
                if t + 2 < N_IN:
                    ring_lo(t + 2)
            pool.wait_ge(z_done, 3 * N_IN)
            g.memset(S0[0:64, HALF:HW], NEG).then_inc(s0_pad, 1)
            g.memset(qbd[:, :, :], 0.0).then_inc(qbd_zero, 1)
            pool.wait_ge(qbd_zero, 1)
            pool.wait_ge(rope_pool, 5)
            for gg in range(4):
                for n in range(2):
                    last = g.tensor_copy(qbd[64 * n:64 * n + 64, :, 32 * n + 8 * gg:32 * n + 8 * gg + 8],
                                         qT[64 * n:64 * n + 64, gg, SEQ:T].rearrange("p (b t) -> p b t", t=DT))
            last.then_inc(qbd_ready, 1)
            pool.wait_ge(qbd_ready, 1)
            for u in range(64):
                n = 128 * (u // 8 + 1)
                pool.wait_ge(ri_done, u + 1)
                g.tensor_scalar(Sx[u % 2][:, 0:n], Sx[u % 2][:, 0:n], ri[:, u % 2:u % 2 + 1], None, ALU.mult).then_inc(norm_done, 1)
            for c, (o, n) in enumerate(CH):
                pool.wait_ge(mix_hi, 2 * c + 1)
                g.tensor_tensor(xn_lo[:, 4:8, o:o + n], convf[:, :, o:o + n], xn_hi[:, 4:8, o:o + n].bitcast(f32), ALU.subtract).then_inc(mixc_ready, 1)
                if c == 0:
                    ring_lo(N_IN)
                    ring_lo(N_IN + 1)
            for w in range(N_IN + 2, N_IN + N_OUT):
                ring_lo(w)
            norm_lo(2)
            ffn(1)
            norm_lo(3)
            pool.wait_ge(pe_hi_done, 1)
            g.tensor_tensor(pe_lo[:, :, :], pe_raw[:, :, :], pe_hi[:, :, :].bitcast(f32), ALU.subtract).then_inc(pe_ready, 1)
            for m in range(N_PLE):
                ring_lo(N_IN + N_OUT + m)
                pool.wait_ge(pp_hi_done, m + 1)
                g.tensor_tensor(pp_lo[m % 2][:, :, :], pp_raw[m % 2][:, :, :], pp_hi[m % 2][:, :, :].bitcast(f32), ALU.subtract).then_inc(pp_ready, 1)

        @block.scalar
        def _(act):
            A = nc.scalar.activation
            act.wait_ge(memset_done, 1)
            act.wait_ge(sel_loaded, 16)
            A(sel[:, :, :].rearrange("p (a b) m -> p a (b m)", a=2), hf[:, 0:2, 0:256], ACT.Copy).then_inc(sel_ready, 1)

            def norm(k):
                for c, (o, n) in enumerate(CH):
                    m = 3 * k + c
                    x_final(act, k, c)
                    if k < 4:
                        wait(act, xn_ready, m)
                    else:
                        wait(act, ssum_done if c else xn_ready, m if c else 12)
                    A(sq[:, :, 0:n], x[:, :, o:o + n], ACT.Square).then_inc(sq_done, 1)
                    act.wait_ge(tot_done, m + 1)
                    A(rms[:, 0:n], ps[:, 7, 0:n], ACT.Sqrt, bias=eps[:, :], scale=1.0 / D).then_inc(rms_done, 1)
                    if k < 4:
                        act.wait_ge(xnf_done, m + 1)
                        A(xn_hi[:, :, o:o + n], sq[:, :, 0:n], ACT.Copy).then_inc(xn_hi_done, 1)

            def ffn(f):
                s_ = F[f]
                with act.Fori(0, PAIRS) as i:
                    for s in range(2):
                        for c, (o, n) in enumerate(CH):
                            u = i * 6 + (3 * s + c)
                            act.wait_ge(s_["gate_done"], u + 1)
                            act.wait_ge(s_["hmul_done"], u + 1)
                            A(silu[:, c, 0:n], ps[:, c, 0:n], ACT.Silu).then_inc(s_["silu_done"], 1)
                            act.wait_ge(s_["hmul_done"], u + 4)
                            act.wait_ge(s_["down_done"], i * 24 + (8 * c + 1))
                            A(h_hi[:, s, o:o + n], hf[:, c, 0:n], ACT.Copy).then_inc(s_["h_hi_done"], 1)

            def ring_hi(w):
                act.wait_ge(wi_loaded[w % 2], 16 * (w // 2 + 1))
                if w < N_IN + N_OUT:
                    wait(act, z_done, 3 * (w - 1))
                else:
                    wait(act, pg_done, 3 * (w - 1 - N_IN - N_OUT))
                A(wi_hi[w % 2][:, :, :], wraw[w % 2][:, :, :], ACT.Copy).then_inc(wi_hi_done, 1)

            def evac(t):
                for c, (o, n) in enumerate(CH):
                    act.wait_ge(z_done, 3 * t + c + 1)
                    z = ps[:, (3 * t + c) % 6, 0:n]
                    if t < T_V:
                        dst, swp = (tb[0], tb[1]) if t % 2 == 0 else (tb[2], tb[3])
                        if c == 0:
                            if t == 0:
                                act.wait_ge(xnf_done, 6)
                                act.wait_ge(x_spilled, 48)
                            elif t <= 4:
                                wait(act, rope_dve, t - 1)
                            else:
                                act.wait_ge(rope_pool, t - 4)
                        A(dst[:, o:o + n], z, ACT.Copy)
                        for q in range(4):
                            last = A(swp[32 * q:32 * q + 32, o:o + n], ps[32 * (q ^ 1):32 * (q ^ 1) + 32, (3 * t + c) % 6, 0:n], ACT.Copy)
                        last.then_inc(z_free, 1)
                    elif t == T_V:
                        A(vT[:, o:o + n], z, ACT.Copy).then_inc(z_free, 1)
                    else:
                        j, part = divmod(t - T_CONV, 3)
                        if c == 0 and part == 0:
                            act.wait_ge(rope_pool, 5)
                            wait(act, conv_done, j)
                        A(tb[part][:, o:o + n], z, ACT.Copy).then_inc(z_free, 1)

            norm(0)
            ffn(0)
            norm(1)
            ring_hi(0)
            act.wait_ge(iw_loaded, 16)
            A(iw_hi[:, :, :], iw_raw[:, :, :], ACT.Copy).then_inc(iw_hi_done, 1)
            ring_hi(1)
            for t in range(3):
                evac(t)
                ring_hi(t + 2)
            q = 0
            act.wait_ge(xn_ready, 6)
            for b in range(2, 8):
                for h in range(4):
                    for o in range(0, 128 * (b + 1), 512):
                        n = min(512, 128 * (b + 1) - o)
                        act.wait_ge(idx_mm, q + 1)
                        wait(act, idx_acc, q - 1)
                        A(rl[:, q % 2, 0:n], ps[:, 6 + q % 2, 0:n], ACT.Relu).then_inc(idx_relu, 1)
                        q += 1
            for t in range(3, N_IN):
                evac(t)
                if t + 2 < N_IN:
                    ring_hi(t + 2)
            for i in range(2):
                act.wait_ge(v_t, i + 1)
                if i == 0:
                    act.wait_ge(iw_done, 1)
                A(V[:, 4 * i:4 * i + 4, :].rearrange("p a b -> p (a b)"), ps[:, 6 + i, :], ACT.Copy).then_inc(v_copied, 1)
            for i in range(2):
                act.wait_ge(v_t, 3 + i)
                A(vn[:, 4 * i:4 * i + 4, :].rearrange("p a b -> p (a b)"), ps[0:DT, 6 + i, :], ACT.Copy).then_inc(v_copied, 1)
            for kc in range(9):
                n = 512 if kc < 8 else DT
                for gr in range(2):
                    act.wait_ge(si_mm, 2 * kc + gr + 1)
                    if gr == 0:
                        wait(act, si_w, kc - 1)
                    A(R[kc % 2][:, gr, 0:n], ps[:, 2 * (kc % 2) + gr, 0:n], ACT.Relu).then_inc(si_relu, 1)
                act.wait_ge(si_w, kc + 1)
                half, o = (kc // 4, (kc % 4) * 512) if kc < 8 else (1, HALF)
                A(S0[64 * half:64 * half + 64, o:o + n], ps[64 * half:64 * half + 64, 4 + kc % 2, 0:n], ACT.Copy).then_inc(si_evac, 1)
            G = 0

            def pt_evac(u, G):
                nblk = u // 8 + 1
                for o in range(0, nblk, 4):
                    k = min(4, nblk - o)
                    act.wait_ge(tr_done, G + 1)
                    if o == 0:
                        wait(act, pv_done, u - 1)
                    A(PT[u % 2][:, o:o + k, :].rearrange("p a b -> p (a b)"), ps[:, 4 + G % 2, 0:128 * k], ACT.Copy).then_inc(pt_done, 1)
                    G += 1
                return G

            for u in range(65):
                if u < 64:
                    n = 128 * (u // 8 + 1)
                    act.wait_ge(nb_done, u + 1)
                    A(Sx[u % 2][:, 0:n], Sx[u % 2][:, 0:n], ACT.Exp, bias=nb[:, u % 2:u % 2 + 1], scale=0.125,
                      accum_out=rs[:, u % 2:u % 2 + 1]).then_inc(exp_done, 1)
                if u >= 1:
                    G = pt_evac(u - 1, G)
            for b in range(NB + 1):
                if b < NB:
                    act.wait_ge(s_nb, b + 1)
                    A(Sa[b % 2][:, :], Sa[b % 2][:, :], ACT.Exp, bias=nb[0:64, b % 2:b % 2 + 1], scale=0.125,
                      accum_out=rs[0:64, b % 2:b % 2 + 1]).then_inc(s_exp, 1)
                if b >= 1:
                    a = b - 1
                    for gr in range(5):
                        act.wait_ge(s_tr, 5 * a + gr + 1)
                        if gr == 0:
                            wait(act, s_pv, a - 1)
                        if gr < 4:
                            A(PTa[a % 2][:, 8 * gr:8 * gr + 8, :].rearrange("p a b -> p (a b)"), ps[:, 4 + (5 * a + gr) % 2, 0:512], ACT.Copy).then_inc(s_pt, 1)
                        else:
                            A(PTa[a % 2][0:DT, PAGES, :], ps[0:DT, 4 + (5 * a + gr) % 2, 0:64], ACT.Copy).then_inc(s_pt, 1)
            act.wait_ge(s_pv, NB)
            act.wait_ge(conv_done, 4)
            for c, (o, n) in enumerate(CH):
                A(xn_hi[:, 4:8, o:o + n], convf[:, :, o:o + n], ACT.Copy).then_inc(mix_hi, 1)
                if c == 0:
                    act.wait_ge(o_done, 32)
                if c == 2:
                    act.wait_ge(s_o, NB)
                A(xn_hi[:, 0:4, o:o + n], attn[:, :, o:o + n], ACT.Copy).then_inc(mix_hi, 1)
                if c == 0:
                    ring_hi(N_IN)
                    ring_hi(N_IN + 1)
            for w in range(N_IN + 2, N_IN + N_OUT):
                ring_hi(w)
            norm(2)
            ffn(1)
            norm(3)
            act.wait_ge(pe_loaded, 16)
            A(pe_hi[:, :, :], pe_raw[:, :, :], ACT.Copy).then_inc(pe_hi_done, 1)

            def ple_hi(m):
                ring_hi(N_IN + N_OUT + m)
                act.wait_ge(pp_loaded[m % 2], 16 * (m // 2 + 1))
                wait(act, pj_done, 3 * (m - 1))
                A(pp_hi[m % 2][:, :, :], pp_raw[m % 2][:, :, :], ACT.Copy).then_inc(pp_hi_done, 1)

            ple_hi(0)
            ple_hi(1)
            for m in range(N_PLE):
                for c, (o, n) in enumerate(CH):
                    act.wait_ge(pg_done, 3 * m + c + 1)
                    wait(act, pmul_done, 3 * (m - 1) + c + 1)
                    A(silu[:, c, 0:n], ps[:, c, 0:n], ACT.Sigmoid).then_inc(sig_done, 1)
                if m + 2 < N_PLE:
                    ple_hi(m + 2)
            norm(4)

        @block.vector
        def _(dve):
            v = nc.vector
            dve.wait_ge(consts_loaded, 16 * 5)

            def norm(k):
                for c, (o, n) in enumerate(CH):
                    m = 3 * k + c
                    dve.wait_ge(sq_done, m + 1)
                    wait(dve, xnf_done, m)
                    v.tensor_reduce(ssum[:, 0:n], sq[:, :, 0:n].rearrange("p k t -> p t k"), axis=AX.X, op=ALU.add).then_inc(ssum_done, 1)
                    dve.wait_ge(rms_done, m + 1)
                    v.reciprocal(ssum[:, 0:n], rms[:, 0:n]).then_inc(recip_done, 1)
                    dve.wait_ge(recip_done, m + 1)
                    out = sq[:, :, 0:n] if k < 4 else y[:, :, o:o + n]
                    for kt in range(KT):
                        last = v.scalar_tensor_tensor(out=out[:, kt, :], in0=x[:, kt, o:o + n], scalar=gain(k, kt),
                                                      in1=ssum[:, 0:n], op0=ALU.mult, op1=ALU.mult)
                    last.then_inc(xnf_done, 1)

            def ffn(f):
                s_ = F[f]
                dve.drain().then_inc(s_["hmul_done"], 3)
                dve.drain().then_inc(s_["acc_done"], 2)
                with dve.Fori(0, PAIRS) as i:
                    for s in range(2):
                        for c, (o, n) in enumerate(CH):
                            u = i * 6 + (3 * s + c)
                            dve.wait_ge(s_["silu_done"], u + 1)
                            dve.wait_ge(s_["up_done"], u + 5)
                            v.tensor_tensor(hf[:, c, 0:n], silu[:, c, 0:n], ps[:, 3 + c, 0:n], ALU.mult).then_inc(s_["hmul_done"], 1)
                            dve.wait_ge(s_["h_hi_done"], u + 1)
                            v.tensor_tensor(h_lo[:, s, o:o + n], hf[:, c, 0:n], h_hi[:, s, o:o + n].bitcast(f32), ALU.subtract).then_inc(s_["h_ready"], 1)
                    for c, (o, n) in enumerate(CH):
                        for m in range(KT):
                            dve.wait_ge(s_["down_done"], i * 24 + (W_READY + 8 * c + m + 1))
                            v.scalar_tensor_tensor(out=x[:, m, o:o + n], in0=ps[:, 6 + m % 2, 0:n], scalar=0.5,
                                                   in1=x[:, m, o:o + n], op0=ALU.mult, op1=ALU.add).then_inc(s_["acc_done"], 1)

            count = {}

            def step(ins, s):
                count[id(s)] = count.get(id(s), 0) + 1
                ins.then_inc(s, 1)
                dve.wait_ge(s, count[id(s)])

            norm(0)
            dve.wait_ge(sel_ready, 1)
            ffn(0)
            norm(1)
            dve.wait_ge(rope_loaded, 16)
            for t in range(3):
                z, zs = (tb[0], tb[1]) if t % 2 == 0 else (tb[2], tb[3])
                dst = iqT[:, t, :] if t < 2 else ikT[:, :]
                dve.wait_ge(z_free, 3 * t + 3)
                v.tensor_tensor(z[:, :], z[:, :], rope[:, 0, :], ALU.mult)
                step(v.tensor_tensor(zs[:, :], zs[:, :], rope[:, 1, :], ALU.mult), rope_step)
                v.tensor_tensor(dst, z[:, :], zs[:, :], ALU.add).then_inc(rope_dve, 1)
            dve.wait_ge(iw_done, 1)
            v.tensor_copy(iw[:, :, :].rearrange("p a b -> p (a b)"), ps[:, 6, 0:36]).then_inc(iw_copied, 1)
            dve.wait_ge(prep_zero, 1)
            dve.wait_ge(rope_dve, 3)
            for h in range(4):
                for b2 in range(2):
                    src = iqT[64 * (h % 2):64 * (h % 2) + 64, h // 2, SEQ:T].rearrange("p (pr b t) -> p pr b t", b=2, t=DT)
                    v.tensor_copy(iqbd[64 * b2:64 * b2 + 64, :, 32 * b2 + 8 * h:32 * b2 + 8 * h + 8], src[:, :, b2, :])
            for b2 in range(2):
                src = ikT[64 * b2:64 * b2 + 64, SEQ:T].rearrange("p (pr b t) -> p pr b t", b=2, t=DT)
                last = v.tensor_copy(ikn[64 * b2:64 * b2 + 64, :, :], src[:, :, b2, :])
            last.then_inc(prep_dve, 1)
            dve.wait_ge(iw_copied, 1)
            for gr in range(2):
                for h in range(4):
                    pick = lambda a: a[:, gr, :].rearrange("p (b h t) -> p b h t", h=4, t=DT)[:, :, h, :]
                    last = v.tensor_scalar(pick(WT), pick(wgt), iw[:, 8, h:h + 1], None, ALU.mult)
            last.then_inc(wt_done, 1)
            dve.wait_ge(xn_ready, 6)
            q = 0
            for b in range(2, 8):
                sc = block_cols(b)
                for h in range(4):
                    for o in range(0, 128 * (b + 1), 512):
                        n = min(512, 128 * (b + 1) - o)
                        dve.wait_ge(idx_relu, q + 1)
                        wait(dve, idx_acc, q)
                        if h == 0:
                            v.tensor_scalar(sc[:, o:o + n], rl[:, q % 2, 0:n], iw[:, b, 0:1], None, ALU.mult).then_inc(idx_acc, 1)
                        else:
                            v.scalar_tensor_tensor(out=sc[:, o:o + n], in0=rl[:, q % 2, 0:n], scalar=iw[:, b, h:h + 1],
                                                   in1=sc[:, o:o + n], op0=ALU.mult, op1=ALU.add).then_inc(idx_acc, 1)
                        q += 1
                dve.wait_ge(idx_acc, q)
                last = v.tensor_tensor(sc[:, 128 * b:], sc[:, 128 * b:], tri, ALU.add)
            last.then_inc(top_step, 1)
            count[id(top_step)] = 1
            dve.wait_ge(wm_t, 1)
            for gr in range(2):
                last = v.tensor_copy(Wm[:, gr, :], ps[:, 6, 128 * gr + 64:128 * gr + 128])
            last.then_inc(wm_ready, 1)
            dve.wait_ge(top_step, 1)
            m0, m1 = block_cols(0), block_cols(1)
            v.tensor_scalar(m0, tri, OFF, None, ALU.max)
            v.memset(m1[:, 0:128], 0.0)
            v.tensor_scalar(m1[:, 128:256], tri, OFF, None, ALU.max)
            for b in range(2, 8):
                sc = block_cols(b)
                with dve.Fori(0, TOPK // 32) as i:
                    for r in range(4):
                        v.max(m8[:, :], sc)
                        dve.drain()
                        v.match_replace(sc, m8[:, :], sc, STRUCK)
                        dve.drain()
                v.tensor_scalar(sc, sc, -3.2e38, OFF, ALU.is_ge, ALU.mult)
            dve.drain()
            dve.wait_ge(si_evac, 9)
            dve.wait_ge(s0_pad, 1)
            step(v.tensor_tensor(S0[64:128, HALF:HW], S0[64:128, HALF:HW], causal8, ALU.add), stop_step)

            def o_evac(k):
                dve.wait_ge(pv_done, 2 * k + 2)
                b, g_ = divmod(k, 4)
                v.tensor_copy(attn[:, g_, 128 * b:128 * b + 128], ps[:, 6 + k % 2, 0:128]).then_inc(o_done, 1)

            groups = [0]
            for u in range(64):
                groups.append(groups[-1] + (u // 8 + 1 + 3) // 4)
            dve.wait_ge(conv_done, 4)
            for u in range(64):
                n = 128 * (u // 8 + 1)
                s = u % 2
                dve.wait_ge(qk_done, u + 1)
                if u >= 2:
                    dve.wait_ge(tr_done, groups[u - 1])
                v.tensor_tensor_reduce(out=Sx[s][:, 0:n], in0=ps[:, 2 * s:2 * s + 2, :].rearrange("p a b -> p (a b)")[:, 0:n],
                                       in1=block_cols(u // 8), scale=1.0, scalar=NEG, op0=ALU.add, op1=ALU.max,
                                       accum_out=mx[:, s:s + 1]).then_inc(smax_done, 1)
                dve.wait_ge(smax_done, u + 1)
                v.tensor_scalar(nb[:, s:s + 1], mx[:, s:s + 1], -0.125, None, ALU.mult).then_inc(nb_done, 1)
                cur = S0 if u < 2 else Wk
                r = u // 2
                if u % 2 == 0:
                    step(v.max(vals[:, 8 * r:8 * r + 8], cur[:, :]), stop_step)
                else:
                    step(v.match_replace(Wk[:, :], vals[:, 8 * r:8 * r + 8], cur[:, :], STRUCK), stop_step)
                dve.wait_ge(exp_done, u + 1)
                v.reciprocal(ri[:, s:s + 1], rs[:, s:s + 1]).then_inc(ri_done, 1)
                if u >= 3 and u % 2 == 1:
                    o_evac((u - 3) // 2)
            st = lambda ins: step(ins, stop_step)
            st(v.tensor_copy(valsB[:, :], vals[64:128, ::-1]))
            st(v.tensor_tensor(valsB[:, :], valsB[:, :], vals[0:64, :], ALU.max))
            st(v.tensor_reduce(tau[0:64, :], valsB[:, :], axis=AX.X, op=ALU.min))
            st(v.tensor_copy(tau[64:128, :], tau[0:64, :]))
            st(v.tensor_scalar(Wk[:, :], S0[:, :], tau[:, :], None, ALU.is_gt, ALU.add, accum_out=cnt[:, 0:1]))
            st(v.tensor_scalar(eqb[:, :], S0[:, :], tau[:, :], None, ALU.is_equal, ALU.add, accum_out=cnt[:, 1:2]))
            v.tensor_copy(cnt[0:64, 2:3], cnt[64:128, 0:1])
            v.tensor_copy(cnt[64:128, 2:3], cnt[0:64, 0:1])
            v.memset(cnt[0:64, 3:4], 0.0)
            st(v.tensor_copy(cnt[64:128, 3:4], cnt[0:64, 1:2]))
            st(v.tensor_tensor(cnt[:, 4:5], cnt[:, 0:1], cnt[:, 2:3], ALU.add))
            st(v.tensor_tensor(cnt[:, 4:5], cnt[:, 4:5], cnt[:, 3:4], ALU.add))
            st(v.tensor_scalar(cnt[:, 5:6], cnt[:, 4:5], -1.0, float(TOPK), ALU.mult, ALU.add))
            st(v.tensor_tensor_scan(cum[:, :], eqb[:, :], eqb[:, :], 0.0, ALU.add, ALU.max))
            st(v.scalar_tensor_tensor(out=cum[:, :], in0=cum[:, :], scalar=cnt[:, 5:6], in1=eqb[:, :], op0=ALU.is_le, op1=ALU.mult))
            st(v.tensor_tensor(Wk[:, :], Wk[:, :], cum[:, :], ALU.add))
            v.tensor_scalar(smask[:, :], Wk[:, :], -1.0, -OFF, ALU.add, ALU.mult).then_inc(smask_ready, 1)
            o_evac(31)

            def s_out(b):
                dve.wait_ge(s_pv, b + 1)
                for n in range(2):
                    last = v.tensor_copy(attn[64 * n:64 * n + 64, :, SEQ + 8 * b:SEQ + 8 * b + 8],
                                         ps[64 * n:64 * n + 64, 6 + b % 2, 32 * n:32 * n + 32].rearrange("p (g t) -> p g t", t=DT))
                last.then_inc(s_o, 1)

            dve.wait_ge(smask_ready, 1)
            for b in range(NB):
                s = b % 2
                for kc in range(9):
                    q = 9 * b + kc
                    n = 512 if kc < 8 else DT
                    dve.wait_ge(s_mm, q + 1)
                    if kc == 0 and b >= 2:
                        dve.wait_ge(s_tr, 5 * (b - 1))
                    v.tensor_scalar(Sa[s][:, 512 * kc:512 * kc + n], ps[0:64, q % 4, 0:n], 1.0, None, ALU.mult, ALU.max,
                                    accum_out=mx9[:, s, kc:kc + 1]).then_inc(s_evac, 1)
                dve.wait_ge(s_evac, 9 * (b + 1))
                v.tensor_reduce(mx[0:64, s:s + 1], mx9[:, s, :], axis=AX.X, op=ALU.max).then_inc(s_mx, 1)
                dve.wait_ge(s_mx, b + 1)
                v.tensor_scalar(nb[0:64, s:s + 1], mx[0:64, s:s + 1], -0.125, None, ALU.mult).then_inc(s_nb, 1)
                dve.wait_ge(s_exp, b + 1)
                v.reciprocal(ri[0:64, s:s + 1], rs[0:64, s:s + 1]).then_inc(s_ri, 1)
                dve.wait_ge(s_ri, b + 1)
                v.tensor_scalar(Sa[s][:, :], Sa[s][:, :], ri[0:64, s:s + 1], None, ALU.mult).then_inc(s_norm, 1)
                if b >= 1:
                    s_out(b - 1)
            s_out(NB - 1)
            for c, (o, n) in enumerate(CH):
                dve.wait_ge(mix_hi, 2 * c + 2)
                v.tensor_tensor(xn_lo[:, 0:4, o:o + n], attn[:, :, o:o + n], xn_hi[:, 0:4, o:o + n].bitcast(f32), ALU.subtract).then_inc(mixa_ready, 1)
            dve.wait_ge(mixa_ready, 3)
            dve.wait_ge(mixc_ready, 3)
            dve.wait_ge(xr_loaded, 16)
            for m in range(N_OUT):
                for c, (o, n) in enumerate(CH):
                    w = N_IN + m
                    dve.wait_ge(z_done, 3 * w + c + 1)
                    v.tensor_tensor(x[:, m, o:o + n], ps[:, (3 * w + c) % 6, 0:n], xr[:, m, o:o + n], ALU.add).then_inc(wo_added, 1)
            norm(2)
            ffn(1)
            norm(3)
            for m in range(N_PLE):
                for c, (o, n) in enumerate(CH):
                    q = 3 * m + c
                    dve.wait_ge(sig_done, q + 1)
                    dve.wait_ge(pj_done, q + 1)
                    v.tensor_tensor(hf[:, c, 0:n], silu[:, c, 0:n], ps[:, 3 + c, 0:n], ALU.mult).then_inc(pmul_done, 1)
                    dve.wait_ge(pmul_done, q + 1)
                    v.tensor_tensor(x[:, m, o:o + n], x[:, m, o:o + n], hf[:, c, 0:n], ALU.add).then_inc(ple_done, 1)
            norm(4)

        @block.tensor
        def _(pe):
            mm = nc.tensor.matmul

            def split_mm(out, hi, lo, mhi, mlo, first, last):
                mm(out, hi, mhi, start=first, stop=False)
                mm(out, hi, mlo, start=False, stop=False)
                return mm(out, lo, mhi, start=False, stop=last)

            def norm(k):
                for c, (o, n) in enumerate(CH):
                    m = 3 * k + c
                    pe.wait_ge(ssum_done, m + 1)
                    mm(ps[:, 7, 0:n], ones[:, :], ssum[:, 0:n], start=True, stop=True).then_inc(tot_done, 1)

            def ffn(f, k):
                s_ = F[f]
                pe.drain().then_inc(s_["down_done"], W_READY)
                pe.drain().then_inc(s_["up_done"], 4)
                for c in range(3):
                    pe.wait_ge(xn_ready, 3 * k + c + 1)
                with pe.Fori(0, PAIRS) as i:
                    for s in range(2):
                        pe.wait_ge(s_["gu_ready"], i * 2 + (s + 2))
                        for c, (o, n) in enumerate(CH):
                            pe.wait_ge(s_["hmul_done"], i * 6 + (3 * s + c + 1))
                            for a, done in ((0, s_["gate_done"]), (1, s_["up_done"])):
                                for kt in range(KT):
                                    last = split_mm(ps[:, 3 * a + c, 0:n], gu_hi[s][:, a, kt, :], gu_lo[s][:, a, kt, :],
                                                    xn_hi[:, kt, o:o + n], xn_lo[:, kt, o:o + n], kt == 0, kt == KT - 1)
                                last.then_inc(done, 1)
                    pe.wait_ge(s_["d_ready"], i * 2 + 3)
                    for c, (o, n) in enumerate(CH):
                        pe.wait_ge(s_["h_ready"], i * 6 + (3 + c + 1))
                        for m in range(KT):
                            pe.wait_ge(s_["acc_done"], i * 24 + (8 * c + m + 1))
                            for s in range(2):
                                last = split_mm(ps[:, 6 + m % 2, 0:n], d_hi[:, s, 128 * m:128 * m + 128], d_lo[:, s, 128 * m:128 * m + 128],
                                                h_hi[:, s, o:o + n], h_lo[:, s, o:o + n], s == 0, s == 1)
                            last.then_inc(s_["down_done"], 1)

            def ring_tile(par, bank0, ready, free):
                ready()
                for c, (o, n) in enumerate(CH):
                    free(c)
                    for kt in range(KT):
                        last = split_mm(ps[:, (bank0 + c) % 6, 0:n], wi_hi[par][:, kt, :], wi_lo[par][:, kt, :],
                                        xn_hi[:, kt, o:o + n], xn_lo[:, kt, o:o + n], kt == 0, kt == KT - 1)
                    last.then_inc(z_done, 1)

            pe.wait_ge(memset_done, 1)
            norm(0)
            ffn(0, 0)
            norm(1)
            for t in range(3):
                def free(c, t=t):
                    if t == 0:
                        pe.wait_ge(xn_ready, 3 + c + 1)
                    wait(pe, z_free, 3 * t + c - 5)
                ring_tile(t % 2, 3 * t, lambda t=t: pe.wait_ge(wi_ready, t + 1), free)
            pe.wait_ge(iw_ready, 1)
            for tt in range(9):
                o = 128 * tt if tt < 8 else T - 128
                for kt in range(KT):
                    last = split_mm(ps[:, 6, 4 * tt:4 * tt + 4], xn_hi[:, kt, o:o + 128], xn_lo[:, kt, o:o + 128],
                                    iw_hi[:, kt, :], iw_lo[:, kt, :], kt == 0, kt == KT - 1)
            last.then_inc(iw_done, 1)
            pe.wait_ge(iw_copied, 1)
            pe.wait_ge(rope_dve, 3)
            pe.wait_ge(rms_done, 6)
            q = 0
            for b in range(2, 8):
                for h in range(4):
                    for o in range(0, 128 * (b + 1), 512):
                        n = min(512, 128 * (b + 1) - o)
                        p0 = 64 * (h % 2)
                        wait(pe, idx_relu, q - 1)
                        mm(ps[:, 6 + q % 2, 0:n], iqT[p0:p0 + 64, h // 2, 128 * b:128 * b + 128], ikT[p0:p0 + 64, o:o + n],
                           start=True, stop=True).then_inc(idx_mm, 1)
                        q += 1
            pe.wait_ge(wt_done, 1)
            pe.wait_ge(idx_relu, q)
            pe.wait_ge(consts_loaded, 16 * 5)
            for gr in range(2):
                last = nc.tensor.transpose(ps[:, 6, 128 * gr:128 * gr + 128], WT[:, gr, :], ident[:, 0, :])
            last.then_inc(wm_t, 1)
            with pe.Fori(0, (N_IN - 3) // 2) as i:
                for e in range(2):
                    t0 = 3 + e
                    ring_tile(t0 % 2, 3 * t0, lambda: pe.wait_ge(wi_ready, i * 2 + (t0 + 1)),
                              lambda c: pe.wait_ge(z_free, i * 6 + (3 * t0 + c - 5)))
            pe.wait_ge(z_free, 3 * T_V + 3)
            pe.wait_ge(wm_ready, 1)
            for i in range(2):
                for j in range(4):
                    last = nc.tensor.transpose(ps[:, 6 + i, 128 * j:128 * j + 128], vT[:, 128 * (4 * i + j):128 * (4 * i + j) + 128], ident[:, 0, :])
                last.then_inc(v_t, 1)
            for i in range(2):
                pe.wait_ge(v_copied, i + 1)
                for j in range(4):
                    o = SEQ + DT * (4 * i + j)
                    last = nc.tensor.transpose(ps[0:DT, 6 + i, 128 * j:128 * j + 128], vT[:, o:o + DT], ident[:, 0, :])
                last.then_inc(v_t, 1)
            pe.wait_ge(z_free, 3 * N_IN)
            pe.wait_ge(prep_dve, 1)
            pe.wait_ge(wm_ready, 1)

            def si_logits(kc):
                n = 512 if kc < 8 else DT
                if kc < 8:
                    pe.wait_ge(idx_loaded[kc % 2], 16 * (kc // 2 + 1))
                for gr in range(2):
                    wait(pe, si_relu, 2 * (kc - 2) + gr + 1)
                    for pr in range(2):
                        rhs = idxp[kc % 2][:, 2 * gr + pr, :] if kc < 8 else ikn[:, 2 * gr + pr, :]
                        last = mm(ps[64 * pr:64 * pr + 64, 2 * (kc % 2) + gr, 0:n], iqbd[:, 2 * gr + pr, :], rhs, start=True, stop=True)
                    last.then_inc(si_mm, 1)

            si_logits(0)
            for kc in range(9):
                if kc < 8:
                    si_logits(kc + 1)
                n = 512 if kc < 8 else DT
                half = kc // 4 if kc < 8 else 1
                pe.wait_ge(si_relu, 2 * kc + 2)
                wait(pe, si_evac, kc - 1)
                for gr in range(2):
                    last = mm(ps[64 * half:64 * half + 64, 4 + kc % 2, 0:n], Wm[:, gr, :], R[kc % 2][:, gr, 0:n], start=gr == 0, stop=gr == 1)
                last.then_inc(si_w, 1)

            pe.wait_ge(rope_pool, 5)
            pe.wait_ge(v_copied, 4)
            pe.wait_ge(si_evac, 9)

            def qk(u):
                b, r = divmod(u, 8)
                g_, n_ = divmod(r, 2)
                wait(pe, smax_done, u - 1)
                for a, o in enumerate(range(0, 128 * (b + 1), 512)):
                    n = min(512, 128 * (b + 1) - o)
                    last = mm(ps[:, 2 * (u % 2) + a, 0:n], qT[64 * n_:64 * n_ + 64, g_, 128 * b:128 * b + 128],
                              kT[64 * n_:64 * n_ + 64, o:o + n], start=True, stop=True)
                last.then_inc(qk_done, 1)

            G = 0
            qk(0)
            for u in range(64):
                b, r = divmod(u, 8)
                g_, n_ = divmod(r, 2)
                if u < 63:
                    qk(u + 1)
                pe.wait_ge(norm_done, u + 1)
                for o in range(0, b + 1, 4):
                    wait(pe, pt_done, G - 1)
                    for j in range(o, min(o + 4, b + 1)):
                        last = nc.tensor.transpose(ps[:, 4 + G % 2, 128 * (j - o):128 * (j - o) + 128], Sx[u % 2][:, 128 * j:128 * j + 128], ident[:, 0, :])
                    last.then_inc(tr_done, 1)
                    G += 1
                pe.wait_ge(pt_done, G)
                wait(pe, o_done, u // 2 - 1)
                for j in range(b + 1):
                    last = mm(ps[64 * n_:64 * n_ + 64, 6 + (u // 2) % 2, 0:128], V[:, j, 64 * n_:64 * n_ + 64], PT[u % 2][:, j, :],
                              start=j == 0, stop=j == b)
                last.then_inc(pv_done, 1)

            pe.wait_ge(qbd_ready, 1)
            pe.wait_ge(kn_ready, 1)
            pe.wait_ge(smax_done, 64)
            pe.wait_ge(smask_ready, 1)

            def s_qk(b):
                pe.wait_ge(kv_loaded[b % 3], 16 * PAGES * (b // 3 + 1))
                for kc in range(9):
                    q = 9 * b + kc
                    n = 512 if kc < 8 else DT
                    half, o = (kc // 4, (kc % 4) * 512) if kc < 8 else (1, HALF)
                    wait(pe, s_evac, q - 3)
                    out = ps[0:64, q % 4, 0:n]
                    rhs = kv[b % 3][:, 4 * kc:4 * kc + 4, 0:128] if kc < 8 else kn[:, DT * b:DT * b + DT]
                    mm(out, qbd[:, b, :], rhs, start=True, stop=False)
                    mm(out, sel[64 * half:64 * half + 64, b, :], smask[64 * half:64 * half + 64, o:o + n], start=False, stop=True).then_inc(s_mm, 1)

            s_qk(0)
            for b in range(NB):
                if b + 1 < NB:
                    s_qk(b + 1)
                pe.wait_ge(s_norm, b + 1)
                for gr in range(5):
                    k = 5 * b + gr
                    wait(pe, s_pt, k - 1)
                    if gr < 4:
                        for j in range(8):
                            last = nc.tensor.transpose(ps[:, 4 + k % 2, 64 * j:64 * j + 64], Sa[b % 2][:, 128 * (8 * gr + j):128 * (8 * gr + j) + 128], ident[0:64, 0, 0:64])
                    else:
                        last = nc.tensor.transpose(ps[0:DT, 4 + k % 2, 0:64], Sa[b % 2][:, PAST:NS], ident[0:64, 0, 0:64])
                    last.then_inc(s_tr, 1)
                wait(pe, s_o, b - 1)
                if b == 0:
                    pe.wait_ge(o_done, 32)
                pe.wait_ge(s_pt, 5 * (b + 1))
                for j in range(PAGES):
                    mm(ps[:, 6 + b % 2, 0:64], kv[b % 3][:, j, 128:256], PTa[b % 2][:, j, :], start=j == 0, stop=False)
                mm(ps[:, 6 + b % 2, 0:64], vn[:, b, :], PTa[b % 2][0:DT, PAGES, :], start=False, stop=True).then_inc(s_pv, 1)

            pe.wait_ge(mixa_ready, 3)
            pe.wait_ge(mixc_ready, 3)
            pe.wait_ge(s_evac, 9 * NB)
            for m in range(N_OUT):
                w = N_IN + m
                ring_tile(w % 2, 3 * w, lambda: pe.wait_ge(wi_ready, w + 1), lambda c: wait(pe, wo_added, 3 * m + c - 5))
            norm(2)
            ffn(1, 2)
            norm(3)
            for m in range(N_PLE):
                w = N_IN + N_OUT + m
                pe.wait_ge(wi_ready, w + 1)
                for c, (o, n) in enumerate(CH):
                    if m == 0:
                        pe.wait_ge(xn_ready, 9 + c + 1)
                    wait(pe, pmul_done, 3 * (m - 1) + c + 1)
                    for kt in range(KT):
                        last = split_mm(ps[:, c, 0:n], wi_hi[w % 2][:, kt, :], wi_lo[w % 2][:, kt, :],
                                        xn_hi[:, kt, o:o + n], xn_lo[:, kt, o:o + n], kt == 0, kt == KT - 1)
                    last.then_inc(pg_done, 1)
                    if c == 0:
                        pe.wait_ge(pp_ready, m + 1)
                        pe.wait_ge(pe_ready, 1)
                    for kt in range(2):
                        last = split_mm(ps[:, 3 + c, 0:n], pp_hi[m % 2][:, kt, :], pp_lo[m % 2][:, kt, :],
                                        pe_hi[:, kt, o:o + n], pe_lo[:, kt, o:o + n], kt == 0, kt == 1)
                    last.then_inc(pj_done, 1)
            norm(4)


def kernel(**inputs):
    import concourse.bacc as bacc
    from concourse.bass_utils import run_bass_kernel_spmd

    f = {k: np.asarray(a) for k, a in inputs.items()}
    nc = bacc.Bacc("TRN2", target_bir_lowering=False, num_devices=1)

    def tokens(prompt, sample, width):
        both = np.concatenate([prompt.reshape(-1, width), sample.reshape(-1, width)])
        return np.ascontiguousarray(both.reshape(T, width // 128, 128).transpose(2, 1, 0))

    def tiles(w):
        return w.reshape(w.shape[0] // 128, 128, -1, 128).transpose(2, 1, 0, 3)

    q0, k0, v0, iq0, ik0, iw0, cb0, cc0, ch0, end = np.cumsum([0, 512, 128, 128, 256, 64, 4, 512, 512, 512])
    head = lambda o, h: list(range(o + 64 * h, o + 64 * h + 64))
    cols = list(range(iq0, ik0)) + head(ik0, 0) * 2 + list(range(k0, v0))
    for g in range(4):
        cols += head(q0, g) + head(q0, 4 + g)
    cols += list(range(v0, iq0))
    for j in range(4):
        for o in (cc0, ch0, cb0):
            cols += list(range(o + 128 * j, o + 128 * j + 128))
    rows = sum((head(0, g) + head(0, 4 + g) for g in range(4)), []) + list(range(512, 1024))
    w_ring = np.ascontiguousarray(np.concatenate([tiles(f["w_in"][0][:, cols]), tiles(f["w_out"][0][rows]), tiles(f["w_ple_gate"][0])]))
    w_iw = np.ascontiguousarray(f["w_in"][0][:, iw0:cb0].reshape(KT, 128, 4).transpose(1, 0, 2))
    w_pp = np.ascontiguousarray(tiles(f["w_ple_proj"][0]))

    p = np.arange(128)
    consts = np.zeros((128, 64), np.float32)
    for k, name in enumerate(("g_ffn1", "g_mix", "g_ffn2", "g_ple", "g_final")):
        consts[:, k * KT:(k + 1) * KT] = f[name].reshape(KT, 128).T
    consts[:, 40:52] = f["conv_w"][0].reshape(3, 4, 128).transpose(2, 1, 0).reshape(128, 12)
    consts[:, 52:60] = np.where(np.arange(8)[None, :] > (p % 8)[:, None], NEG, 0)
    ident = np.stack([np.eye(128), np.where(p[None, :] > p[:, None], NEG, 0)], 1).astype(np.float32)
    c64 = np.arange(64)
    sel = ((p % 64 // 8)[:, None, None] == np.arange(8)[None, :, None]) & ((p % 8)[:, None, None] == (c64 % 8)[None, None, :])
    sel = sel.astype(np.float32).reshape(128, 2, 256)
    col = np.arange(128)
    wg = np.stack([(p >= 64)[:, None] & (((p - 64) // 8)[:, None] == (4 * gr + col // 32)[None, :]) & ((p % 8)[:, None] == (col % 8)[None, :])
                   for gr in range(2)], 1).astype(np.float32)
    inv = np.float32(10000.0) ** (-np.arange(32, dtype=np.float32) / np.float32(32))
    pos = np.concatenate([np.arange(SEQ), np.tile(PAST + np.arange(DT), NB)]).astype(np.float32)
    ang = pos[None, :] * inv[p % 32][:, None]
    rope = np.stack([np.cos(ang), np.sin(ang) * np.where(p % 64 < 32, -1, 1)[:, None].astype(np.float32)], 1).astype(np.float32)

    pages_kT = f["cache_k"][0].transpose(0, 2, 3, 1).reshape(NPOOL, 128, PAGE)
    arrays = {
        "x_in": tokens(f["x_prompt"], f["x_sample"], D),
        "consts": consts, "ident_tri": ident, "sel": sel, "wgt_sel": wg,
        "page_table": np.ascontiguousarray(f["page_table"].reshape(1, -1)),
        "rope_tab": np.ascontiguousarray(rope),
        "w1_gu": np.ascontiguousarray(np.stack([f["w1_gate"][0], f["w1_up"][0]]).reshape(2, KT, 128, FT, 128).transpose(3, 2, 0, 1, 4)),
        "w1_d": f["w1_down"][0].reshape(FT, 128, D),
        "w2_gu": np.ascontiguousarray(np.stack([f["w2_gate"][0], f["w2_up"][0]]).reshape(2, KT, 128, FT, 128).transpose(3, 2, 0, 1, 4)),
        "w2_d": f["w2_down"][0].reshape(FT, 128, D),
        "w_ring": w_ring, "w_iw": w_iw, "w_pp": w_pp,
        "idx_pages": np.ascontiguousarray(f["cache_idx_k"][0].transpose(0, 2, 1)),
        "kv_pages": np.ascontiguousarray(np.concatenate([pages_kT, f["cache_v"][0].reshape(NPOOL, PAGE, 128)], 2)),
        "p_in": tokens(f["p_prompt"], f["p_sample"], 256),
        "conv_state": np.ascontiguousarray(f["state_conv"][0].reshape(NB, 2, 4, 128).transpose(3, 2, 0, 1)),
    }
    t = {k: nc.dram_tensor("in_" + k, a.shape, mybir.dt.from_np(a.dtype), kind="ExternalInput").ap() for k, a in arrays.items()}
    outs = {"y": (128, KT, T), "k": (128, T), "v": (128, T), "ik": (64, T), "conv": (128, 4, 18)}
    o = {k: nc.dram_tensor("out_" + k, s, f32, kind="ExternalOutput").ap() for k, s in outs.items()}
    x_spill = nc.dram_tensor("x_spill", (128, KT, T), f32, kind="Internal").ap()
    idx_flat = nc.dram_tensor("idx_flat", (NB, 64, PAST), f32, kind="Internal").ap()
    program(nc, t["x_in"], t["consts"], t["ident_tri"], t["sel"], t["wgt_sel"], t["page_table"], t["rope_tab"],
            (t["w1_gu"], t["w2_gu"]), (t["w1_d"], t["w2_d"]), t["w_ring"], t["w_iw"], t["w_pp"], t["idx_pages"], t["kv_pages"],
            (t["p_in"], t["conv_state"]), o["y"], o["k"], o["v"], o["ik"], o["conv"], x_spill, idx_flat)
    res = run_bass_kernel_spmd(nc, [{"in_" + k: a for k, a in arrays.items()}], core_ids=[0]).results[0]
    y = res["out_y"].transpose(2, 1, 0).reshape(T, D)
    k, v, ik = (res["out_" + n].T for n in ("k", "v", "ik"))
    conv = res["out_conv"]
    cp = conv[:, :, 0:2].transpose(2, 1, 0).reshape(1, 1, 2, 512)
    cs = conv[:, :, 2:18].reshape(128, 4, NB, 2).transpose(2, 3, 1, 0).reshape(1, NB, 2, 512)
    return (y[:SEQ].reshape(1, SEQ, D), y[SEQ:].reshape(NB, DT, D),
            k[:SEQ].reshape(1, 1, SEQ, 2, 64), v[:SEQ].reshape(1, 1, SEQ, 2, 64), ik[:SEQ].reshape(1, 1, SEQ, 64), cp,
            k[SEQ:].reshape(1, NB, DT, 2, 64), v[SEQ:].reshape(1, NB, DT, 2, 64), ik[SEQ:].reshape(1, NB, DT, 64), cs)
```
